# Optimizing a Trainium2 kernel written in Bass

```python
import math
import numpy as np
import jax
import jax.numpy as jnp
from jax import lax

D_MODEL = 1024
BATCH = 1
SEQ = 2048
DEPTH = 2

CHUNK = 64
Q_BLOCK = 128
HEAD_DIM = 64
MIX_WIDTH = D_MODEL

SB_HEADS = 6
SB_WIDTH = SB_HEADS * HEAD_DIM
CA_HEADS = 6
CA_WIDTH = CA_HEADS * HEAD_DIM
CA_LEFT_CHUNKS = 8
CA_BAND = (CA_LEFT_CHUNKS + 1) * CHUNK
MAX_REL = 256
DA_HEADS = 4
DA_VDIM = 64
DA_QKDIM = 32
DA_WIDTH = DA_HEADS * DA_VDIM

IN_WIDTH = 4 * (SB_WIDTH + CA_WIDTH + DA_WIDTH)
ROPE_THETA = 10000.0
EPS = 1e-6

kernel_name = "hybrid_stickbreak_chunkrel_diffattn_block"

def rmsnorm(x, g):
    xf = x.astype(jnp.float32)
    y = xf * lax.rsqrt(jnp.mean(xf * xf, axis=-1, keepdims=True) + EPS)
    return (y * g.astype(jnp.float32)).astype(x.dtype)

def rotary(x, positions):
    d = x.shape[-1]
    half = d // 2
    inv_freq = ROPE_THETA ** (-np.arange(half, dtype=np.float32) / half)
    ang = positions.astype(jnp.float32)[..., None] * inv_freq
    ang = ang.reshape(ang.shape[:2] + (1,) * (x.ndim - 3) + (half,))
    cos, sin = jnp.cos(ang), jnp.sin(ang)
    xf = x.astype(jnp.float32)
    x1, x2 = xf[..., :half], xf[..., half:]
    return jnp.concatenate([x1 * cos - x2 * sin, x2 * cos + x1 * sin], axis=-1).astype(x.dtype)

def stick_breaking_attention(q, k, v):
    _, _, s_len, d = q.shape
    scale = d ** -0.5
    outs = []
    for i in range(s_len // Q_BLOCK):
        lo, hi = i * Q_BLOCK, (i + 1) * Q_BLOCK
        z = jnp.einsum('bhqd,bhkd->bhqk', q[:, :, lo:hi], k[:, :, :hi]).astype(jnp.float32) * scale
        strict = np.arange(hi)[None, :] < np.arange(lo, hi)[:, None]
        log_1m_beta = jnp.where(strict, jax.nn.log_sigmoid(-z), 0.0)
        between = lax.cumsum(log_1m_beta, axis=3, reverse=True) - log_1m_beta
        w = jnp.where(strict, jnp.exp(jax.nn.log_sigmoid(z) + between), 0.0)
        outs.append(jnp.einsum('bhqk,bhkd->bhqd', w.astype(v.dtype), v[:, :, :hi]))
    return jnp.concatenate(outs, axis=2)

def chunk_relpos_attention(q, k, v, rel_table):
    b, h, s_len, d = q.shape
    nc = s_len // CHUNK
    scale = d ** -0.5
    qc = q.reshape(b, h, nc, CHUNK, d)
    pad = ((0, 0), (0, 0), (CA_LEFT_CHUNKS * CHUNK, 0), (0, 0))
    kc = jnp.pad(k, pad).reshape(b, h, nc + CA_LEFT_CHUNKS, CHUNK, d)
    vc = jnp.pad(v, pad).reshape(b, h, nc + CA_LEFT_CHUNKS, CHUNK, d)
    k_band = jnp.concatenate([kc[:, :, o:o + nc] for o in range(CA_LEFT_CHUNKS + 1)], axis=3)
    v_band = jnp.concatenate([vc[:, :, o:o + nc] for o in range(CA_LEFT_CHUNKS + 1)], axis=3)
    scores = jnp.einsum('bhcqd,bhckd->bhcqk', qc, k_band).astype(jnp.float32) * scale
    rel = (CA_LEFT_CHUNKS * CHUNK + np.arange(CHUNK)[:, None]) - np.arange(CA_BAND)[None, :]
    rel_idx = np.clip(rel, -MAX_REL, MAX_REL) + MAX_REL
    bias = rel_table.astype(jnp.float32)[:, rel_idx]
    key_chunk = np.arange(nc)[:, None] - CA_LEFT_CHUNKS + (np.arange(CA_BAND) // CHUNK)[None, :]
    valid = key_chunk >= 0
    scores = jnp.where(valid[None, None, :, None, :], scores + bias[None, :, None], -jnp.inf)
    probs = jax.nn.softmax(scores, axis=-1).astype(v.dtype)
    out = jnp.einsum('bhcqk,bhckd->bhcqd', probs, v_band)
    return out.reshape(b, h, s_len, d)

def diff_attention(q, k, v, lam, lam_init, subln_g):
    _, _, _, s_len, dk = q.shape
    scale = dk ** -0.5
    outs = []
    for i in range(s_len // Q_BLOCK):
        lo, hi = i * Q_BLOCK, (i + 1) * Q_BLOCK
        s = jnp.einsum('bhnqd,bhnkd->bhnqk', q[:, :, :, lo:hi], k[:, :, :, :hi]).astype(jnp.float32) * scale
        mask = (np.arange(hi) // CHUNK)[None, :] <= (np.arange(lo, hi) // CHUNK)[:, None]
        p = jax.nn.softmax(jnp.where(mask, s, -jnp.inf), axis=-1)
        w = p[:, :, 0] - lam * p[:, :, 1]
        outs.append(jnp.einsum('bhqk,bhkd->bhqd', w.astype(v.dtype), v[:, :, :hi]))
    o = jnp.concatenate(outs, axis=2)
    return rmsnorm(o, subln_g) * (1.0 - lam_init)

def hybrid_layer(x, positions, w_in, w_out, pre_g, post_g, rel_table,
                 lq1, lk1, lq2, lk2, subln_g, lam_init):
    b, s_len, _ = x.shape
    h = rmsnorm(x, pre_g)
    proj = h @ w_in
    a_part = proj[..., :4 * SB_WIDTH]
    b_part = proj[..., 4 * SB_WIDTH:4 * (SB_WIDTH + CA_WIDTH)]
    c_part = proj[..., 4 * (SB_WIDTH + CA_WIDTH):]

    def heads(t, n):
        return t.reshape(b, s_len, n, -1).transpose(0, 2, 1, 3)

    def merge(t):
        return t.transpose(0, 2, 1, 3).reshape(b, s_len, -1)

    qa, ka, va, ga = jnp.split(a_part, 4, axis=-1)
    ya = stick_breaking_attention(heads(qa, SB_HEADS), heads(ka, SB_HEADS), heads(va, SB_HEADS))
    ya = merge(ya) * jax.nn.silu(ga)

    qb, kb, vb, gb = jnp.split(b_part, 4, axis=-1)
    yb = chunk_relpos_attention(heads(qb, CA_HEADS), heads(kb, CA_HEADS), heads(vb, CA_HEADS), rel_table)
    yb = merge(yb) * jax.nn.silu(gb)

    qc, kc, vc, gc = jnp.split(c_part, 4, axis=-1)
    qc = rotary(qc.reshape(b, s_len, DA_HEADS, 2, DA_QKDIM), positions).transpose(0, 2, 3, 1, 4)
    kc = rotary(kc.reshape(b, s_len, DA_HEADS, 2, DA_QKDIM), positions).transpose(0, 2, 3, 1, 4)
    lam = (jnp.exp(jnp.sum(lq1.astype(jnp.float32) * lk1.astype(jnp.float32)))
           - jnp.exp(jnp.sum(lq2.astype(jnp.float32) * lk2.astype(jnp.float32))) + lam_init)
    yc = diff_attention(qc, kc, heads(vc, DA_HEADS), lam, lam_init, subln_g)
    yc = merge(yc) * jax.nn.silu(gc)

    y = jnp.concatenate([ya, yb, yc], axis=-1) @ w_out
    return x + rmsnorm(y, post_g)

def setup_inputs(seed: int = 0) -> dict:
    key = jax.random.key(seed)
    ks = jax.random.split(key, 12)
    x = jax.random.normal(ks[0], (BATCH, SEQ, D_MODEL), jnp.float32)
    positions = jnp.broadcast_to(jnp.arange(SEQ, dtype=jnp.int32), (BATCH, SEQ))
    w_in = jax.random.normal(ks[1], (DEPTH, D_MODEL, IN_WIDTH), jnp.float32) * D_MODEL ** -0.5
    w_out = jax.random.normal(ks[2], (DEPTH, MIX_WIDTH, D_MODEL), jnp.float32) * MIX_WIDTH ** -0.5
    pre_gain = 1.0 + 0.02 * jax.random.normal(ks[3], (DEPTH, D_MODEL), jnp.float32)
    post_gain = 1.0 + 0.02 * jax.random.normal(ks[4], (DEPTH, D_MODEL), jnp.float32)
    rel_bias = 0.1 * jax.random.normal(ks[5], (DEPTH, CA_HEADS, 2 * MAX_REL + 1), jnp.float32)
    lambda_q1 = 0.1 * jax.random.normal(ks[6], (DEPTH, DA_QKDIM), jnp.float32)
    lambda_k1 = 0.1 * jax.random.normal(ks[7], (DEPTH, DA_QKDIM), jnp.float32)
    lambda_q2 = 0.1 * jax.random.normal(ks[8], (DEPTH, DA_QKDIM), jnp.float32)
    lambda_k2 = 0.1 * jax.random.normal(ks[9], (DEPTH, DA_QKDIM), jnp.float32)
    subln_gain = 1.0 + 0.02 * jax.random.normal(ks[10], (DEPTH, DA_VDIM), jnp.float32)
    return {"x": x, "positions": positions, "w_in": w_in, "w_out": w_out,
            "pre_gain": pre_gain, "post_gain": post_gain, "rel_bias": rel_bias,
            "lambda_q1": lambda_q1, "lambda_k1": lambda_k1, "lambda_q2": lambda_q2,
            "lambda_k2": lambda_k2, "subln_gain": subln_gain}

def reference(x, positions, w_in, w_out, pre_gain, post_gain, rel_bias,
              lambda_q1, lambda_k1, lambda_q2, lambda_k2, subln_gain):
    for layer in range(DEPTH):
        lam_init = 0.8 - 0.6 * math.exp(-0.3 * layer)
        x = hybrid_layer(x, positions, w_in[layer], w_out[layer], pre_gain[layer], post_gain[layer],
                         rel_bias[layer], lambda_q1[layer], lambda_k1[layer], lambda_q2[layer],
                         lambda_k2[layer], subln_gain[layer], lam_init)
    return x


_drawn_inputs = setup_inputs


def setup_inputs(seed=0):
    import zlib

    import numpy as np

    out = dict(_drawn_inputs(seed))
    spreads = {}
    factors = {'rel_bias': 6.623, 'lambda_q1': 6.429, 'subln_gain': 3.189}
    for name, (base, spread) in spreads.items():
        noise = np.random.default_rng([zlib.crc32(name.encode()), seed]).standard_normal(out[name].shape)
        drawn = base * np.exp(spread * noise) if base else spread * noise
        out[name] = jnp.asarray(drawn.astype(out[name].dtype))
    for name, factor in factors.items():
        out[name] = (out[name] * factor).astype(out[name].dtype)
    return out
```

```python
import math
from collections import namedtuple
from contextlib import ExitStack, contextmanager

import numpy as np

import concourse.bass as bass
from concourse import mybir

F32 = mybir.dt.float32
F32R = mybir.dt.float32r
BF16 = mybir.dt.bfloat16
I32 = mybir.dt.int32
ALU = mybir.AluOpType
ACT = mybir.ActivationFunctionType
AX = mybir.AxisListType.X

P = 128
ROPE_FREQ = [np.float32(10000.0) ** np.float32(-np.float32(j) / np.float32(16)) for j in range(16)]
TURN_PARTS = (6.28125, 0.001934051513671875, 1.255422830581665e-06, 2.430837753308879e-10)
EXP_LN = "natural_log_exp_and_others"
BIG = 1.0e30
LOWEST = -3.0e38
EPS = 1e-6
ROPE_THETA = 10000.0
MAGIC = 12582912.0


def trunk(nc, x, positions, w_pairs, w_out, pre_gain, post_gain, rel_bias,
          lq1, lk1, lq2, lk2, subln_gain, out):
    SEQ, D = x.shape
    DEPTH, PAIRS, _, KC, PW = w_pairs.shape
    TILES = SEQ // P
    HD = PW // 8
    CA_HEADS, TABLE = rel_bias.shape[1:]
    MAX_REL = (TABLE - 1) // 2
    DK = lq1.shape[1]
    HALF = DK // 2
    CHUNK = 64
    BAND = 5 * P
    EXT = BAND + P - 1
    SB_SCALE = HD ** -0.5
    DA_SCALE = DK ** -0.5
    SB_PAIRS, CA_PAIRS = 3, CA_HEADS // 2
    N = 512

    xs = nc.dram_tensor("xs", (DEPTH + 1, SEQ, D), F32).ap()
    proj = nc.dram_tensor("proj", (PAIRS, SEQ, PW), F32).ap()
    ymix = nc.dram_tensor("ymix", (SEQ, D), F32).ap()
    skew = nc.dram_tensor("skew", (DEPTH * CA_HEADS, P * EXT), F32).ap()
    layer_par = nc.dram_tensor("layer_par", (DEPTH, P, 1 + HD), F32).ap()

    with ExitStack() as top:
        def sb(name, shape, dt=F32, where=top):
            return where.enter_context(nc.sbuf_tensor(name, shape, dt))

        @contextmanager
        def phase(*names):
            with ExitStack() as held:
                sems = [held.enter_context(nc.semaphore(n)) for n in names]
                yield namedtuple("Semaphores", names)(*sems)
                nums = sorted(s.num for s in sems)
                assert nums == list(range(nums[0], nums[0] + len(nums)))
                nc.gpsimd.sem_clear(range(nums[0], nums[-1] + 1))
                nc.all_engine_barrier(sem_only=True)

        ps = top.enter_context(nc.psum_tensor("ps", [P, 8, N], F32))
        ident = sb("ident", [P, P])
        identb = sb("identb", [P, P], BF16)
        strict_mask = sb("strict_mask", [P, P], BF16)
        chunk_mask = sb("chunk_mask", [P, P], BF16)
        cos = sb("cos", [P, TILES, HALF])
        sin = sb("sin", [P, TILES, HALF])
        eps = sb("eps", [P, 1])

        with ExitStack() as scope, phase("loaded", "copied", "consts", "angle", "trig", "ext", "skewed",
                                         "lam", "lam_exp", "par", "par_out") as s:
            zeros = sb("zeros", [P, P], F32, scope)
            pos_i = sb("pos_i", [P, TILES], I32, scope)
            pos = sb("pos", [P, TILES], F32, scope)
            ang = sb("ang", [P, TILES, HALF], F32, scope)
            turns = sb("turns", [P, TILES, HALF], F32, scope)
            red = sb("red", [P, 2, TILES, HALF], F32, scope)
            table = sb("table", [P, DEPTH * CA_HEADS, TABLE], F32, scope)
            ext = sb("ext", [P, DEPTH * CA_HEADS, EXT], F32, scope)
            lam_in = sb("lam_in", [P, 4, DEPTH, DK], F32, scope)
            lam_mul = sb("lam_mul", [P, DK], F32, scope)
            lam_sum = sb("lam_sum", [P, DEPTH, 2], F32, scope)
            par = sb("par_all", [P, DEPTH, 1 + HD], F32, scope)
            gain = sb("gain", [P, DEPTH, HD], F32, scope)
            with nc.Block() as block:
                @block.sync
                def _(sp):
                    sp.dma_start(xs[0], x).then_inc(s.copied, 16)
                    with nc.allow_non_contiguous_dma(reason="one position per row, once"):
                        sp.dma_start(pos_i[:, :], positions.rearrange("(t p) -> p t", p=P)).then_inc(s.loaded, 16)
                    for i, a in enumerate((lq1, lk1, lq2, lk2)):
                        sp.dma_start(lam_in[:, i], a.unsqueeze(0).to_broadcast([P, DEPTH, DK])).then_inc(s.loaded, 16)
                    sp.dma_start(gain[:, :, :], subln_gain.unsqueeze(0).to_broadcast([P, DEPTH, HD])).then_inc(s.loaded, 16)
                    sp.dma_start(table[:, :, :], rel_bias.rearrange("l h n -> (l h) n").unsqueeze(0)
                                 .to_broadcast([P, DEPTH * CA_HEADS, TABLE])).then_inc(s.loaded, 16)
                    for n in range(DEPTH * CA_HEADS):
                        sp.wait_ge(s.ext, 2 * (n + 1))
                        sp.dma_start(skew[n].rearrange("(p e) -> p e", p=P), ext[:, n]).then_inc(s.skewed, 16)
                    sp.wait_ge(s.par, 2 * DEPTH)
                    sp.dma_start(layer_par.rearrange("l p c -> p l c"), par[:, :, :]).then_inc(s.par_out, 16)
                    sp.wait_ge(s.skewed, 16 * DEPTH * CA_HEADS)
                    sp.wait_ge(s.par_out, 16)
                    sp.wait_ge(s.copied, 16)

                @block.gpsimd
                def _(pool):
                    nc.gpsimd.memset(zeros[:, :], 0.0).then_inc(s.consts, 1)
                    nc.gpsimd.memset(eps[:, :], EPS).then_inc(s.consts, 1)
                    nc.gpsimd.memset(chunk_mask[:, :], 0.0).then_inc(s.consts, 1)
                    pool.wait_ge(s.consts, 3)
                    nc.gpsimd.memset(chunk_mask[0:CHUNK, CHUNK:P], -BIG).then_inc(s.consts, 1)
                    for m in (ident, identb):
                        nc.gpsimd.affine_select(out=m[:, :], in_=zeros[:, :], compare_op=ALU.not_equal, fill=1.0,
                                                base=0, pattern=[[-1, P]], channel_multiplier=1).then_inc(s.consts, 1)
                    nc.gpsimd.affine_select(out=strict_mask[:, :], in_=zeros[:, :], compare_op=ALU.is_ge, fill=-BIG,
                                            base=-1, pattern=[[-1, P]], channel_multiplier=1).then_inc(s.consts, 1)

                @block.vector
                def _(dve):
                    dve.wait_ge(s.loaded, 16 * 7)
                    nc.vector.tensor_copy(pos[:, :], pos_i[:, :]).then_inc(s.angle, 1)
                    dve.wait_ge(s.angle, 1)
                    for j in range(HALF):
                        inv = float(ROPE_FREQ[j])
                        nc.vector.tensor_scalar(ang[:, :, j], pos[:, :], inv, None, ALU.mult).then_inc(s.angle, 1)
                    done = 1 + HALF
                    dve.wait_ge(s.angle, done)
                    nc.vector.tensor_scalar(turns[:, :, :], ang[:, :, :], 1.0 / (2 * math.pi), MAGIC,
                                            ALU.mult, ALU.add).then_inc(s.angle, 1)
                    dve.wait_ge(s.angle, done + 1)
                    nc.vector.tensor_scalar(turns[:, :, :], turns[:, :, :], MAGIC, None, ALU.subtract).then_inc(s.angle, 1)
                    done += 2
                    src = ang[:, :, :]
                    for part in TURN_PARTS:
                        dve.wait_ge(s.angle, done)
                        nc.vector.scalar_tensor_tensor(out=red[:, 0], in0=turns[:, :, :], scalar=-part, in1=src,
                                                       op0=ALU.mult, op1=ALU.add).then_inc(s.angle, 1)
                        src = red[:, 0]
                        done += 1
                    dve.wait_ge(s.angle, done)
                    nc.vector.tensor_scalar(red[:, 1], red[:, 0], math.pi / 2, None, ALU.add).then_inc(s.angle, 1)
                    dve.wait_ge(s.angle, done + 1)
                    nc.vector.tensor_scalar(turns[:, :, :], red[:, 1], math.pi, -2 * math.pi,
                                            ALU.is_gt, ALU.mult).then_inc(s.angle, 1)
                    dve.wait_ge(s.angle, done + 2)
                    nc.vector.tensor_tensor(red[:, 1], red[:, 1], turns[:, :, :], ALU.add).then_inc(s.angle, 1)
                    dve.wait_ge(s.angle, done + 3)
                    nc.vector.tensor_scalar(red[:, :, :, :], red[:, :, :, :], 3.1415925, -3.1415925,
                                            ALU.min, ALU.max).then_inc(s.trig, 1)
                    for n in range(DEPTH * CA_HEADS):
                        flat = BAND - 1 - MAX_REL + 1
                        nc.vector.tensor_scalar(ext[:, n, 0:flat], table[:, n, TABLE - 1:TABLE].to_broadcast([P, flat]),
                                                0.0, None, ALU.add).then_inc(s.ext, 1)
                        rest = EXT - flat
                        nc.vector.tensor_copy(ext[:, n, flat:EXT],
                                              table[:, n, TABLE - 1 - rest:TABLE - 1][:, ::-1]).then_inc(s.ext, 1)
                    for l in range(DEPTH):
                        for j in range(2):
                            nc.vector.tensor_tensor_reduce(lam_mul[:, :], lam_in[:, 2 * j, l], lam_in[:, 2 * j + 1, l], 1.0,
                                                           0.0, ALU.mult, ALU.add, lam_sum[:, l, j:j + 1]).then_inc(s.lam, 1)
                            dve.wait_ge(s.lam, 2 * l + j + 1)
                    dve.wait_ge(s.lam_exp, 1)
                    for l in range(DEPTH):
                        lam_init = 0.8 - 0.6 * math.exp(-0.3 * l)
                        nc.vector.tensor_tensor(par[:, l, 0:1], lam_sum[:, l, 1:2], lam_sum[:, l, 0:1],
                                                ALU.subtract).then_inc(s.lam, 1)
                        dve.wait_ge(s.lam, 2 * DEPTH + l + 1)
                        nc.vector.tensor_scalar(par[:, l, 0:1], par[:, l, 0:1], lam_init, None,
                                                ALU.subtract).then_inc(s.par, 1)
                        nc.vector.tensor_scalar(par[:, l, 1:], gain[:, l], 1.0 - lam_init, None,
                                                ALU.mult).then_inc(s.par, 1)

                @block.scalar
                def _(act):
                    act.wait_ge(s.trig, 1)
                    nc.scalar.activation(sin[:, :, :], red[:, 0], ACT.Sin)
                    nc.scalar.activation(cos[:, :, :], red[:, 1], ACT.Sin)
                    act.wait_ge(s.lam, 2 * DEPTH)
                    nc.scalar.activation(lam_sum[:, :, :], lam_sum[:, :, :], ACT.Exp).then_inc(s.lam_exp, 1)

        with nc.Fori(0, DEPTH) as layer:
            with ExitStack() as scope:
                h_hi = sb("h_hi", [P, KC, SEQ], F32R, scope)
                h_lo = sb("h_lo", [P, KC, SEQ], F32R, scope)
                w_raw = sb("w_raw", [P, KC, PW], F32, scope)
                with ExitStack() as inner, phase("gain_in", "x_in0", "x_in1", "sq", "ms", "rstd", "h", "ht", "hi", "lo", "w_in") as s:
                    gain = sb("pre", [P, D], F32, inner)
                    xt = sb("xt", [P, 2, D], F32, inner)
                    ht = sb("ht", [P, 2, D], F32, inner)
                    st = sb("st", [P, 2, 2], F32, inner)
                    with nc.Block() as block:
                        @block.sync
                        def _(sp):
                            sp.dma_start(gain[:, :], pre_gain[layer].unsqueeze(0).to_broadcast([P, D])).then_inc(s.gain_in, 16)
                            for t in range(TILES):
                                if t >= 2:
                                    sp.wait_ge(s.h, t - 1)
                                sp.dma_start(xt[:, t % 2], xs[layer, t * P:(t + 1) * P, :]).then_inc((s.x_in0, s.x_in1)[t % 2], 16)
                                if t == 1:
                                    sp.dma_start(w_raw[:, :, :], w_pairs[layer, 0]).then_inc(s.w_in, 16)
                            sp.wait_ge(s.w_in, 16)

                        @block.scalar
                        def _(act):
                            act.preload_act_table_set(EXP_LN)
                            for t in range(TILES + 1):
                                if t < TILES:
                                    act.wait_ge((s.x_in0, s.x_in1)[t % 2], 16 * (t // 2 + 1))
                                    if t >= 2:
                                        act.wait_ge(s.ht, t - 1)
                                    nc.scalar.activation(ht[:, t % 2], xt[:, t % 2], ACT.Square,
                                                         accum_out=st[:, t % 2, 0:1]).then_inc(s.sq, 1)
                                    act.wait_ge(s.sq, t + 1)
                                    nc.scalar.activation(st[:, t % 2, 1:2], st[:, t % 2, 0:1], ACT.Ln, scale=1.0 / D,
                                                         bias=eps[:, :]).then_inc(s.ms, 1)
                                    act.wait_ge(s.ms, t + 1)
                                    nc.scalar.activation(st[:, t % 2, 1:2], st[:, t % 2, 1:2], ACT.Exp,
                                                         scale=-0.5).then_inc(s.rstd, 1)
                                if t >= 1:
                                    act.wait_ge(s.ht, t)
                                    b = 2 * ((t - 1) % 2)
                                    for j in range(2):
                                        nc.scalar.activation(h_hi[:, 4 * j:4 * j + 4, (t - 1) * P:t * P],
                                                             ps[:, b + j, :].rearrange("p (k n) -> p k n", k=4),
                                                             ACT.Copy).then_inc(s.hi, 1)

                        @block.vector
                        def _(dve):
                            dve.wait_ge(s.gain_in, 16)
                            for t in range(TILES + 1):
                                if t < TILES:
                                    dve.wait_ge(s.rstd, t + 1)
                                    nc.vector.scalar_tensor_tensor(out=ht[:, t % 2], in0=xt[:, t % 2],
                                                                   scalar=st[:, t % 2, 1:2], in1=gain[:, :],
                                                                   op0=ALU.mult, op1=ALU.mult).then_inc(s.h, 1)
                                if t >= 1:
                                    b = 2 * ((t - 1) % 2)
                                    for j in range(2):
                                        dve.wait_ge(s.hi, 2 * (t - 1) + j + 1)
                                        hs = h_hi[:, 4 * j:4 * j + 4, (t - 1) * P:t * P].bitcast(F32)
                                        nc.vector.tensor_tensor(h_lo[:, 4 * j:4 * j + 4, (t - 1) * P:t * P],
                                                                ps[:, b + j, :].rearrange("p (k n) -> p k n", k=4),
                                                                hs, ALU.subtract).then_inc(s.lo, 1)

                        @block.tensor
                        def _(pe):
                            for t in range(TILES):
                                pe.wait_ge(s.h, t + 1)
                                if t >= 2:
                                    pe.wait_ge(s.lo, 2 * (t - 1))
                                for k in range(KC):
                                    last = nc.tensor.transpose(ps[:, 2 * (t % 2) + k // 4, (k % 4) * P:(k % 4 + 1) * P],
                                                               ht[:, t % 2, k * P:(k + 1) * P], ident[:, :])
                                last.then_inc(s.ht, 1)

                w_hi = sb("w_hi", [P, KC, PW], F32R, scope)
                w_lo = sb("w_lo", [P, KC, PW], F32R, scope)
                stage = sb("stage", [P, 4, PW], F32, scope)
                with nc.Fori(0, PAIRS) as pair:
                    with phase("w_hi_done", "w_lo_done", "acc", "ev_act", "ev_dve", "w_in", "out0", "out1", "out2", "out3") as s:
                        outs = (s.out0, s.out1, s.out2, s.out3)
                        with nc.Block() as block:
                            @block.sync
                            def _(sp):
                                sp.wait_ge(s.w_lo_done, KC)
                                sp.dma_start(w_raw[:, :, :], w_pairs[layer, (pair + 1) % PAIRS]).then_inc(s.w_in, 16)
                                for t in range(TILES):
                                    sp.wait_ge((s.ev_act, s.ev_dve)[t % 2], t // 2 + 1)
                                    sp.dma_start(proj[pair, t * P:(t + 1) * P, :], stage[:, t % 4]).then_inc(
                                        outs[t % 4], 16)
                                for stored in outs:
                                    sp.wait_ge(stored, 16 * TILES // 4)
                                sp.wait_ge(s.w_in, 16)

                            @block.scalar
                            def _(act):
                                for k in range(KC):
                                    nc.scalar.activation(w_hi[:, k], w_raw[:, k], ACT.Copy).then_inc(s.w_hi_done, 1)
                                for t in range(0, TILES, 2):
                                    act.wait_ge(s.acc, t + 1)
                                    if t >= 4:
                                        act.wait_ge(outs[t % 4], 16 * (t // 4))
                                    nc.scalar.activation(stage[:, t % 4], ps[:, t % 4, :], ACT.Copy).then_inc(s.ev_act, 1)

                            @block.vector
                            def _(dve):
                                for k in range(KC):
                                    dve.wait_ge(s.w_hi_done, k + 1)
                                    nc.vector.tensor_tensor(w_lo[:, k], w_raw[:, k], w_hi[:, k].bitcast(F32),
                                                            ALU.subtract).then_inc(s.w_lo_done, 1)
                                for t in range(1, TILES, 2):
                                    dve.wait_ge(s.acc, t + 1)
                                    if t >= 4:
                                        dve.wait_ge(outs[t % 4], 16 * (t // 4))
                                    nc.vector.tensor_copy(stage[:, t % 4], ps[:, t % 4, :]).then_inc(s.ev_dve, 1)

                            @block.tensor
                            def _(pe):
                                for t in range(TILES):
                                    if t >= 4:
                                        pe.wait_ge((s.ev_act, s.ev_dve)[t % 2], t // 2 - 1)
                                    tok = slice(t * P, (t + 1) * P)
                                    for k in range(KC):
                                        if t == 0:
                                            pe.wait_ge(s.w_lo_done, k + 1)
                                        acc = ps[:, t % 4, :]
                                        nc.tensor.matmul(acc, h_hi[:, k, tok], w_hi[:, k], start=(k == 0), stop=False)
                                        nc.tensor.matmul(acc, h_hi[:, k, tok], w_lo[:, k], start=False, stop=False)
                                        last = nc.tensor.matmul(acc, h_lo[:, k, tok], w_hi[:, k], start=False,
                                                                stop=(k == KC - 1))
                                    last.then_inc(s.acc, 1)

            with ExitStack() as scope:
                raw = sb("raw", [P, TILES, PW], F32, scope)
                val = sb("val", [P, TILES, P], F32, scope)
                gate = sb("gate", [P, TILES, P], F32, scope)
                ybuf = sb("ybuf", [P, TILES, P], F32, scope)
                wt = sb("wt", [P, 4, N], F32, scope)
                operand = sb("operand", [P, 8, SEQ], F32R, scope)
                parts = sb("parts", [P, 2, 4, 4, P], F32, scope)

                def pair_rows(pair):
                    return proj[pair].rearrange("(t p) n -> p t n", p=P)

                with phase("raw_in") as s:
                    with nc.Block() as block:
                        @block.sync
                        def _(sp):
                            sp.dma_start(raw[:, :, :], pair_rows(0)).then_inc(s.raw_in, 16)
                            sp.wait_ge(s.raw_in, 16)

                PREP = ("g_exp", "g_add", "g_rec", "g_done", "v_done", "rot_pool", "rot_dve", "hi_done", "lo_done",
                        "tr", "op_act", "op_dve", "raw_in", "extra_in", "extra", "y_out")
                UNITS = 8

                class Prep:

                    def __init__(self, s, builds, per):
                        self.s, self.builds, self.per = s, builds, per
                        self.on_act = [k for k in range(per) if k % 2 == 0]
                        self.on_dve = [k for k in range(per) if k % 2 == 1]
                        self.count = len(builds(0, 0, parts[:, 0]))

                    def reload(self, sp, pair_next):
                        sp.wait_ge(self.s.lo_done, self.count * UNITS)
                        sp.wait_ge(self.s.v_done, 1)
                        sp.wait_ge(self.s.g_done, 1)
                        sp.dma_start(raw[:, :, :], pair_rows(pair_next)).then_inc(self.s.raw_in, 16)

                    def pool(self):
                        nc.gpsimd.tensor_copy(val[:, :, :], raw[:, :, 2 * P:3 * P]).then_inc(self.s.v_done, 1)

                    def act(self, act):
                        s = self.s
                        for u in range(UNITS + 1):
                            if u < UNITS:
                                if u >= 2:
                                    act.wait_ge(s.tr, u - 1)
                                for hi, lo, src, ref, scale in self.builds(u // 4, u % 4, parts[:, u % 2]):
                                    nc.scalar.activation(hi.bitcast(F32R), src, ACT.Copy, scale=scale).then_inc(s.hi_done, 1)
                            if u >= 1:
                                act.wait_ge(s.tr, u)
                                for k in self.on_act:
                                    self.evacuate(nc.scalar.copy, u - 1, k).then_inc(s.op_act, 1)

                    def dve(self, dve):
                        s = self.s
                        for u in range(UNITS + 1):
                            if u < UNITS:
                                for i, (hi, lo, src, ref, scale) in enumerate(self.builds(u // 4, u % 4, parts[:, u % 2])):
                                    dve.wait_ge(s.hi_done, u * self.count + i + 1)
                                    if scale == 1.0:
                                        nc.vector.tensor_tensor(lo.bitcast(F32R), src, ref, ALU.subtract).then_inc(s.lo_done, 1)
                                    else:
                                        nc.vector.scalar_tensor_tensor(out=lo.bitcast(F32R), in0=src, scalar=scale, in1=ref,
                                                                       op0=ALU.mult, op1=ALU.subtract).then_inc(s.lo_done, 1)
                            if u >= 1:
                                dve.wait_ge(s.tr, u)
                                for k in self.on_dve:
                                    self.evacuate(nc.vector.tensor_copy, u - 1, k).then_inc(s.op_dve, 1)

                    def evacuate(self, copy, u, k):
                        return copy(operand[:, (u // 4) * self.per + k, (u % 4) * N:(u % 4 + 1) * N],
                                    ps[:, 4 * (u % 2) + k, :])

                    def gate_act(self, act):
                        nc.scalar.activation(gate[:, :, :], raw[:, :, 3 * P:4 * P], ACT.Exp, scale=-1.0).then_inc(self.s.g_exp, 1)

                    def gate_dve(self, dve):
                        s = self.s
                        dve.wait_ge(s.g_exp, 1)
                        nc.vector.tensor_scalar(gate[:, :, :], gate[:, :, :], 1.0, None, ALU.add).then_inc(s.g_add, 1)
                        dve.wait_ge(s.g_add, 1)
                        nc.vector.reciprocal(gate[:, :, :], gate[:, :, :]).then_inc(s.g_rec, 1)
                        dve.wait_ge(s.g_rec, 1)
                        nc.vector.tensor_tensor(gate[:, :, :], gate[:, :, :], raw[:, :, 3 * P:4 * P],
                                                ALU.mult).then_inc(s.g_done, 1)

                    def pe(self, pe):
                        s = self.s
                        for u in range(UNITS):
                            pe.wait_ge(s.lo_done, self.count * (u + 1))
                            if u >= 2:
                                pe.wait_ge(s.op_act, len(self.on_act) * (u - 1))
                                pe.wait_ge(s.op_dve, len(self.on_dve) * (u - 1))
                            for k in range(self.per):
                                for t in range(4):
                                    last = nc.tensor.transpose(ps[:, 4 * (u % 2) + k, t * P:(t + 1) * P],
                                                               parts[:, u % 2, t, k], ident[:, :])
                            last.then_inc(s.tr, 1)
                        pe.wait_ge(s.op_act, len(self.on_act) * UNITS)
                        pe.wait_ge(s.op_dve, len(self.on_dve) * UNITS)
                        pe.wait_ge(s.v_done, 1)

                def rep(a):
                    return a.unsqueeze(2).to_broadcast([P, a.shape[1], 2, a.shape[2]])

                def wide_builds(scale):
                    def builds(h, g, part):
                        tiles = slice(4 * g, 4 * g + 4)
                        q = raw[:, tiles, h * HD:(h + 1) * HD]
                        k = rep(raw[:, tiles, P + h * HD:P + (h + 1) * HD])
                        k_hi = part[:, :, 1].rearrange("p t (r n) -> p t r n", r=2)
                        k_lo = part[:, :, 2].rearrange("p t (r n) -> p t r n", r=2)
                        return [(part[:, :, 0, 0:HD], part[:, :, 0, HD:], q, part[:, :, 0, 0:HD], scale),
                                (k_hi, k_lo, k, k_hi, 1.0)]
                    return builds

                def narrow_builds(h, g, part):
                    tiles = slice(4 * g, 4 * g + 4)
                    found = []
                    for m in range(2):
                        at = h * HD + m * DK
                        q = part[:, :, 2 * m].rearrange("p t (r b n) -> p t b r n", r=2, b=2)
                        k = part[:, :, 2 * m + 1].rearrange("p t (b r n) -> p t b r n", r=2, b=2)
                        found.append((q[:, :, 0], q[:, :, 1], rep(raw[:, tiles, at:at + DK]), q[:, :, 0], 1.0))
                        found.append((k[:, :, 0], k[:, :, 1], rep(raw[:, tiles, P + at:P + at + DK]), k[:, :, 0], 1.0))
                    return found

                def store(sp, s, pair, done, count):
                    sp.wait_ge(done, count)
                    sp.dma_start(ymix[:, bass.ds(pair * P, P)].rearrange("(t p) n -> p t n", p=P), ybuf[:, :, :]).then_inc(s.y_out, 16)
                    sp.wait_ge(s.y_out, 16)
                    sp.wait_ge(s.raw_in, 16)

                items = [(h, i) for h in range(2) for i in range(TILES)]

                with ExitStack() as inner:
                    soft = sb("soft", [P, 3, N], F32, inner)
                    cum = sb("cum", [P, 2, N], F32, inner)
                    wgt = sb("wgt", [P, 4, N], F32, inner)
                    chunks = [(n, h, i, c, min(N, P * (i + 1) - N * c)) for n, (h, i) in enumerate(items)
                              for c in reversed(range((P * (i + 1) + N - 1) // N))]
                    CH = len(chunks)
                    first = [x == 0 or chunks[x - 1][0] != chunks[x][0] for x in range(CH)]
                    final = [x == CH - 1 or chunks[x + 1][0] != chunks[x][0] for x in range(CH)]
                    with nc.Fori(0, SB_PAIRS) as pair:
                        with phase(*PREP, "z", "absz", "ez", "lnz", "sp", "cum", "arg", "w", "wtr", "wt_act", "wt_dve",
                                   "av", "y") as s:
                            prep = Prep(s, wide_builds(SB_SCALE), 3)
                            with nc.Block() as block:
                                @block.sync
                                def _(sp):
                                    prep.reload(sp, pair + 1)
                                    store(sp, s, pair, s.y, len(items))

                                @block.gpsimd
                                def _(pool):
                                    prep.pool()

                                @block.scalar
                                def _(act):
                                    act.preload_act_table_set(EXP_LN)
                                    prep.gate_act(act)
                                    prep.act(act)
                                    for x in range(CH + 3):
                                        if x < CH:
                                            w = chunks[x][4]
                                            act.wait_ge(s.z, x + 1)
                                            if x >= 3:
                                                act.wait_ge(s.cum, x - 2)
                                            nc.scalar.activation(soft[:, x % 3, 0:w], ps[:, x % 4, 0:w], ACT.Abs).then_inc(s.absz, 1)
                                        if 2 <= x < CH + 2:
                                            m = x - 2
                                            act.wait_ge(s.arg, m + 1)
                                            v = wgt[:, m % 4, 0:chunks[m][4]]
                                            nc.scalar.activation(v, v, ACT.Exp).then_inc(s.w, 1)
                                        if x < CH:
                                            w = chunks[x][4]
                                            v = soft[:, x % 3, 0:w]
                                            act.wait_ge(s.absz, x + 1)
                                            nc.scalar.activation(v, v, ACT.Exp, scale=-1.0).then_inc(s.ez, 1)
                                        if x >= 3 and x % 2 == 1:
                                            m = x - 3
                                            w = chunks[m][4]
                                            act.wait_ge(s.wtr, m + 1)
                                            if m >= 4:
                                                act.wait_ge(s.av, m - 3)
                                            nc.scalar.copy(wt[:, m % 4, 0:w], ps[:, 4, 0:w]).then_inc(s.wt_act, 1)
                                        if x < CH:
                                            w = chunks[x][4]
                                            v = soft[:, x % 3, 0:w]
                                            act.wait_ge(s.ez, x + 1)
                                            nc.scalar.activation(v, v, ACT.Ln, bias=1.0).then_inc(s.lnz, 1)

                                @block.vector
                                def _(dve):
                                    prep.dve(dve)
                                    prep.gate_dve(dve)
                                    dve.wait_ge(s.g_done, 1)
                                    for x in range(CH + 4):
                                        if x < CH:
                                            w = chunks[x][4]
                                            z = ps[:, x % 4, 0:w]
                                            v = soft[:, x % 3, 0:w]
                                            dve.wait_ge(s.lnz, x + 1)
                                            nc.vector.scalar_tensor_tensor(out=v, in0=z, scalar=0.0, in1=v, op0=ALU.max,
                                                                           op1=ALU.add).then_inc(s.sp, 1)
                                            dve.wait_ge(s.sp, x + 1)
                                            carry = 0.0
                                            if x >= 1:
                                                dve.wait_ge(s.cum, x)
                                                if not first[x]:
                                                    carry = cum[:, (x - 1) % 2, 0:1]
                                            if x >= 2:
                                                dve.wait_ge(s.arg, x - 1)
                                            back = v[:, ::-1]
                                            nc.vector.tensor_tensor_scan(cum[:, x % 2, 0:w][:, ::-1], back, back, carry,
                                                                         ALU.add, ALU.max).then_inc(s.cum, 1)
                                            dve.wait_ge(s.cum, x + 1)
                                            if x >= 4:
                                                dve.wait_ge(s.wtr, x - 3)
                                            nc.vector.tensor_tensor(wgt[:, x % 4, 0:w], z, cum[:, x % 2, 0:w],
                                                                    ALU.subtract).then_inc(s.arg, 1)
                                        if 3 <= x < CH + 3 and x % 2 == 0:
                                            m = x - 3
                                            w = chunks[m][4]
                                            dve.wait_ge(s.wtr, m + 1)
                                            if m >= 4:
                                                dve.wait_ge(s.av, m - 3)
                                            nc.vector.tensor_copy(wt[:, m % 4, 0:w], ps[:, 5, 0:w]).then_inc(s.wt_dve, 1)
                                        if x >= 4 and final[x - 4]:
                                            n, h, i, c, w = chunks[x - 4]
                                            dve.wait_ge(s.av, x - 3)
                                            cols = slice(h * HD, (h + 1) * HD)
                                            nc.vector.tensor_tensor(ybuf[:, i, cols], ps[:, 6 + n % 2, 0:HD], gate[:, i, cols],
                                                                    ALU.mult).then_inc(s.y, 1)

                                @block.tensor
                                def _(pe):
                                    prep.pe(pe)
                                    for x in range(-1, CH + 4):
                                        if x + 1 < CH:
                                            n, h, i, c, w = chunks[x + 1]
                                            if x >= 3:
                                                pe.wait_ge(s.arg, x - 2)
                                            z = ps[:, (x + 1) % 4, 0:w]
                                            q = operand[:, 3 * h, i * P:(i + 1) * P]
                                            keys = slice(N * c, N * c + w)
                                            nc.tensor.matmul(z, q, operand[:, 3 * h + 1, keys], start=True, stop=False)
                                            if first[x + 1]:
                                                nc.tensor.matmul(z[:, w - P:w], identb[:, :], strict_mask[:, :],
                                                                 start=False, stop=False)
                                            last = nc.tensor.matmul(z, q, operand[:, 3 * h + 2, keys], start=False, stop=True)
                                            last.then_inc(s.z, 1)
                                        if x >= 4:
                                            m = x - 4
                                            n, h, i, c, w = chunks[m]
                                            pe.wait_ge((s.wt_act, s.wt_dve)[m % 2], m // 2 + 1)
                                            if first[m] and n >= 2:
                                                pe.wait_ge(s.y, n - 1)
                                            for b in range(w // P):
                                                last = nc.tensor.matmul(ps[:, 6 + n % 2, 0:HD], wt[:, m % 4, b * P:(b + 1) * P],
                                                                        val[:, 4 * c + b, h * HD:(h + 1) * HD],
                                                                        start=(first[m] and b == 0),
                                                                        stop=(final[m] and b == w // P - 1))
                                            last.then_inc(s.av, 1)
                                        if 2 <= x < CH + 2:
                                            m = x - 2
                                            w = chunks[m][4]
                                            pe.wait_ge(s.w, m + 1)
                                            if m >= 2:
                                                pe.wait_ge((s.wt_act, s.wt_dve)[m % 2], m // 2)
                                            for b in range(w // P):
                                                last = nc.tensor.transpose(ps[:, 4 + m % 2, b * P:(b + 1) * P],
                                                                           wgt[:, m % 4, b * P:(b + 1) * P], ident[:, :])
                                            last.then_inc(s.wtr, 1)

                with ExitStack() as inner:
                    bias = sb("bias", [P, 2, BAND], F32, inner)
                    prob = sb("prob", [P, 3, BAND], F32, inner)
                    top_s = sb("top_s", [P, 4, 4], F32, inner)
                    units = []
                    for n, (h, i) in enumerate(items):
                        nb = min(i, 4) + 1
                        for b0 in range(0, nb, 4):
                            units.append((n, h, i, b0, min(4, nb - b0), nb))
                    of_item = [[u for u, unit in enumerate(units) if unit[0] == n] for n in range(len(items))]
                    with nc.Fori(0, CA_PAIRS) as pair:
                        with phase(*PREP, "sc", "bmax", "nmax", "pr", "rsum", "wtr", "wt_act", "wt_dve", "av", "y") as s:
                            prep = Prep(s, wide_builds(SB_SCALE), 3)
                            with nc.Block() as block:
                                @block.sync
                                def _(sp):
                                    for h in range(2):
                                        band = skew[layer * CA_HEADS + pair * 2 + h][P - 1:P - 1 + P * (EXT - 1)]
                                        sp.dma_start(bias[:, h], band.rearrange("(p e) -> p e", p=P)[:, 0:BAND]).then_inc(s.extra_in, 16)
                                    prep.reload(sp, pair + SB_PAIRS + 1)
                                    store(sp, s, pair + SB_PAIRS, s.y, len(items))

                                @block.gpsimd
                                def _(pool):
                                    prep.pool()
                                    pool.wait_ge(s.extra_in, 32)
                                    pool.wait_ge(s.v_done, 1)
                                    nc.gpsimd.memset(bias[0:CHUNK, :, BAND - CHUNK:BAND], -BIG).then_inc(s.extra, 1)
                                    nc.gpsimd.memset(bias[CHUNK:P, :, 0:CHUNK], -BIG).then_inc(s.extra, 1)

                                @block.scalar
                                def _(act):
                                    act.preload_act_table_set(EXP_LN)
                                    prep.gate_act(act)
                                    prep.act(act)
                                    for n in range(len(items) + 2):
                                        if n < len(items):
                                            L = P * units[of_item[n][0]][5]
                                            act.wait_ge(s.nmax, n + 1)
                                            e = prob[:, n % 3, 0:L]
                                            nc.scalar.activation(e, e, ACT.Exp, bias=top_s[:, n % 4, 1:2],
                                                                 accum_out=top_s[:, n % 4, 2:3]).then_inc(s.pr, 1)
                                        if 1 <= n <= len(items):
                                            for u in of_item[n - 1]:
                                                if u % 2 == 0:
                                                    w = units[u][4] * P
                                                    act.wait_ge(s.wtr, u + 1)
                                                    if u >= 4:
                                                        act.wait_ge(s.av, u - 3)
                                                    nc.scalar.copy(wt[:, u % 4, 0:w], ps[:, 4, 0:w]).then_inc(s.wt_act, 1)

                                @block.vector
                                def _(dve):
                                    prep.dve(dve)
                                    prep.gate_dve(dve)
                                    dve.wait_ge(s.g_done, 1)
                                    dve.wait_ge(s.extra, 2)
                                    for n in range(len(items) + 2):
                                        if n < len(items):
                                            L = P * units[of_item[n][0]][5]
                                            bank = 2 * (n % 2)
                                            dve.wait_ge(s.sc, n + 1)
                                            if n >= 3:
                                                dve.wait_ge(s.wtr, of_item[n - 3][-1] + 1)
                                            sc = ps[:, bank:bank + 2, :].rearrange("p b n -> p (b n)")[:, 0:L]
                                            nc.vector.tensor_tensor_reduce(prob[:, n % 3, 0:L], sc, bias[:, items[n][0], BAND - L:BAND],
                                                                           1.0, LOWEST, ALU.add, ALU.max,
                                                                           top_s[:, n % 4, 0:1]).then_inc(s.bmax, 1)
                                            dve.wait_ge(s.bmax, n + 1)
                                            nc.vector.tensor_scalar(top_s[:, n % 4, 1:2], top_s[:, n % 4, 0:1], -1.0, None,
                                                                    ALU.mult).then_inc(s.nmax, 1)
                                        if 1 <= n <= len(items):
                                            for u in of_item[n - 1]:
                                                if u % 2 == 1:
                                                    w = units[u][4] * P
                                                    dve.wait_ge(s.wtr, u + 1)
                                                    if u >= 4:
                                                        dve.wait_ge(s.av, u - 3)
                                                    nc.vector.tensor_copy(wt[:, u % 4, 0:w], ps[:, 5, 0:w]).then_inc(s.wt_dve, 1)
                                        if n >= 2:
                                            m = n - 2
                                            h, i = items[m]
                                            dve.wait_ge(s.pr, m + 1)
                                            nc.vector.reciprocal(top_s[:, m % 4, 3:4], top_s[:, m % 4, 2:3]).then_inc(s.rsum, 1)
                                            dve.wait_ge(s.rsum, m + 1)
                                            dve.wait_ge(s.av, of_item[m][-1] + 1)
                                            cols = slice(h * HD, (h + 1) * HD)
                                            nc.vector.scalar_tensor_tensor(out=ybuf[:, i, cols], in0=ps[:, 6 + m % 2, 0:HD],
                                                                           scalar=top_s[:, m % 4, 3:4], in1=gate[:, i, cols],
                                                                           op0=ALU.mult, op1=ALU.mult).then_inc(s.y, 1)

                                @block.tensor
                                def _(pe):
                                    prep.pe(pe)

                                    def values(u):
                                        n, h, i, b0, blocks, nb = units[u]
                                        pe.wait_ge((s.wt_act, s.wt_dve)[u % 2], u // 2 + 1)
                                        if b0 == 0 and n >= 2:
                                            pe.wait_ge(s.y, n - 1)
                                        for b in range(blocks):
                                            last = nc.tensor.matmul(ps[:, 6 + n % 2, 0:HD], wt[:, u % 4, b * P:(b + 1) * P],
                                                                    val[:, i + 1 - nb + b0 + b, h * HD:(h + 1) * HD],
                                                                    start=(b0 + b == 0), stop=(b0 + b == nb - 1))
                                        last.then_inc(s.av, 1)

                                    for n in range(-1, len(items) + 2):
                                        if n + 1 < len(items):
                                            h, i = items[n + 1]
                                            nb = min(i, 4) + 1
                                            k0, L = P * (i + 1 - nb), P * nb
                                            if n >= 1:
                                                pe.wait_ge(s.bmax, n)
                                            q = operand[:, 3 * h, i * P:(i + 1) * P]
                                            for c in range(0, L, N):
                                                w = min(N, L - c)
                                                sc = ps[:, 2 * ((n + 1) % 2) + c // N, 0:w]
                                                nc.tensor.matmul(sc, q, operand[:, 3 * h + 1, k0 + c:k0 + c + w], start=True, stop=False)
                                                last = nc.tensor.matmul(sc, q, operand[:, 3 * h + 2, k0 + c:k0 + c + w],
                                                                        start=False, stop=True)
                                            last.then_inc(s.sc, 1)
                                        if n >= 2:
                                            for u in of_item[n - 2]:
                                                values(u)
                                        if 1 <= n <= len(items):
                                            for u in of_item[n - 1]:
                                                _, h, i, b0, blocks, nb = units[u]
                                                pe.wait_ge(s.pr, n)
                                                if u >= 2:
                                                    pe.wait_ge((s.wt_act, s.wt_dve)[u % 2], u // 2)
                                                for b in range(blocks):
                                                    last = nc.tensor.transpose(ps[:, 4 + u % 2, b * P:(b + 1) * P],
                                                                               prob[:, (n - 1) % 3, (b0 + b) * P:(b0 + b + 1) * P],
                                                                               ident[:, :])
                                                last.then_inc(s.wtr, 1)

                with ExitStack() as inner:
                    ex = sb("ex", [P, 2, 2, SEQ], F32, inner)
                    par = sb("par", [P, 1 + HD], F32, inner)
                    chunk_max = sb("chunk_max", [P, 2, 2, 4], F32, inner)
                    shift = sb("shift", [P, 2, 2, 2], F32, inner)
                    part_sum = sb("part_sum", [P, 2, 2, 4], F32, inner)
                    sums = sb("sums", [P, 8, 6], F32, inner)
                    o1 = sb("o1", [P, 4, HD], F32, inner)
                    o2 = sb("o2", [P, 4, HD], F32, inner)
                    norm = sb("norm", [P, 4, 2], F32, inner)
                    nch = [(i + 4) // 4 for h, i in items]
                    T = len(items)
                    maps = [(n, m, c) for n in range(T) for m in range(2) for c in range(nch[n])]
                    index = {key: a for a, key in enumerate(maps)}
                    units = [(n, c) for n in range(T) for c in range(nch[n])]
                    uindex = {key: u for u, key in enumerate(units)}

                    def width(n, c):
                        return min(N, P * (items[n][1] + 1) - N * c)

                    def order():
                        late = {"copy": [], "value": []}
                        ended = []

                        def after_turn(c, n):
                            found = [("turn", n, 0, c)]
                            for kind, behind in (("copy", 1), ("value", 2)):
                                late[kind].append((kind, n, 0, c))
                                if len(late[kind]) > behind:
                                    found.append(late[kind].pop(0))
                                    if kind == "value" and found[-1][3] == nch[found[-1][1]] - 1:
                                        ended.append(found[-1][1])
                            return found
                        for n in range(T + 3):
                            lanes = [[], [], []]
                            if n < T:
                                for m in range(2):
                                    lanes[0] += [("max", n, m, c) for c in range(nch[n])] + [("shift", n, m, 0)]
                            if 1 <= n <= T:
                                lanes[1] += [("exp", n - 1, m, c) for m in range(2) for c in range(nch[n - 1])]
                            if 2 <= n <= T + 1:
                                lanes[2].append(("ratio", n - 2, 0, 0))
                                for c in range(nch[n - 2]):
                                    lanes[2].append(("weigh", n - 2, 0, c))
                                    if c >= 1:
                                        lanes[2] += after_turn(c - 1, n - 2)
                                lanes[2] += after_turn(nch[n - 2] - 1, n - 2)
                            if n == T + 2:
                                lanes[2] += late["copy"] + late["value"]
                                ended.append(T - 1)
                            while ended:
                                m = ended.pop(0)
                                at = max([k for k, e in enumerate(lanes[2]) if e[0] == "value" and e[1] == m])
                                for j, kind in enumerate(("norm", "root", "gated")):
                                    lanes[2].insert(min(at + 2 + 2 * j, len(lanes[2])), (kind, m, 0, 0))
                            while any(lanes):
                                for lane in lanes:
                                    if lane:
                                        yield lane.pop(0)
                    steps = list(order())

                    with nc.Fori(0, PAIRS - SB_PAIRS - CA_PAIRS) as pair:
                        with phase(*PREP, "mx", "rmax", "cmax", "sm", "ex", "tot", "rec", "ratio", "wg", "wtr", "wt_act",
                                   "wt_dve", "av", "o1", "ss", "lnn", "rs", "y") as s:
                            prep = Prep(s, narrow_builds, 4)

                            def rotary(j):
                                v = raw[:, :, j * P:(j + 1) * P].rearrange("p t (b f n) -> p t b f n", f=2, n=HALF)
                                room = ex[:, j].rearrange("p m (r t b n) -> p (m r) t b n", r=2, t=TILES, b=4)
                                return v[:, :, :, 0], v[:, :, :, 1], room
                            shape = [P, TILES, 4, HALF]
                            cos_b = cos[:, :, :].unsqueeze(2).to_broadcast(shape)
                            sin_b = sin[:, :, :].unsqueeze(2).to_broadcast(shape)

                            with nc.Block() as block:
                                @block.sync
                                def _(sp):
                                    sp.dma_start(par[:, :], layer_par[layer]).then_inc(s.extra_in, 16)
                                    prep.reload(sp, pair * -1 + (PAIRS - 1))
                                    store(sp, s, pair + (SB_PAIRS + CA_PAIRS), s.y, T)

                                @block.gpsimd
                                def _(pool):
                                    for j in range(2):
                                        x1, x2, room = rotary(j)
                                        nc.gpsimd.tensor_tensor(room[:, 1], x2, sin_b, ALU.mult).then_inc(s.rot_pool, 1)
                                        nc.gpsimd.tensor_tensor(room[:, 2], x1, sin_b, ALU.mult).then_inc(s.rot_pool, 1)
                                    prep.pool()

                                @block.scalar
                                def _(act):
                                    act.preload_act_table_set(EXP_LN)
                                    prep.gate_act(act)
                                    act.wait_ge(s.rot_dve, 8)
                                    prep.act(act)
                                    for kind, n, m, c in steps:
                                        w = width(n, c)
                                        if kind == "exp":
                                            a = index[n, m, c]
                                            act.wait_ge(s.ex, a + 1)
                                            act.wait_ge(s.sm, 2 * n + m + 1)
                                            if n >= 2:
                                                act.wait_ge(s.wtr, uindex[n - 2, nch[n - 2] - 1] + 1)
                                            nc.scalar.activation(ex[:, n % 2, m, N * c:N * c + w], ps[:, 2 + a % 3, 0:w], ACT.Exp,
                                                                 bias=shift[:, n % 2, m, 1:2], scale=DA_SCALE,
                                                                 accum_out=part_sum[:, n % 2, m, c:c + 1]).then_inc(s.cmax, 1)
                                        elif kind == "copy" and uindex[n, c] % 2 == 0:
                                            u = uindex[n, c]
                                            act.wait_ge(s.wtr, u + 1)
                                            if u >= 4:
                                                act.wait_ge(s.av, u - 3)
                                            nc.scalar.copy(wt[:, u % 4, 0:w], ps[:, 5, 0:w]).then_inc(s.wt_act, 1)
                                        elif kind == "root":
                                            act.wait_ge(s.ss, n + 1)
                                            nc.scalar.activation(norm[:, n % 4, 1:2], norm[:, n % 4, 0:1], ACT.Ln, scale=1.0 / HD,
                                                                 bias=eps[:, :]).then_inc(s.lnn, 1)
                                            act.wait_ge(s.lnn, n + 1)
                                            nc.scalar.activation(norm[:, n % 4, 1:2], norm[:, n % 4, 1:2], ACT.Exp,
                                                                 scale=-0.5).then_inc(s.rs, 1)

                                @block.vector
                                def _(dve):
                                    for j in range(2):
                                        x1, x2, room = rotary(j)
                                        nc.vector.tensor_tensor(room[:, 0], x1, cos_b, ALU.mult).then_inc(s.rot_dve, 1)
                                        nc.vector.tensor_tensor(room[:, 3], x2, cos_b, ALU.mult).then_inc(s.rot_dve, 1)
                                        dve.wait_ge(s.rot_pool, 2 * j + 2)
                                        dve.wait_ge(s.rot_dve, 4 * j + 2)
                                        nc.vector.tensor_tensor(x1, room[:, 0], room[:, 1], ALU.subtract).then_inc(s.rot_dve, 1)
                                        nc.vector.tensor_tensor(x2, room[:, 2], room[:, 3], ALU.add).then_inc(s.rot_dve, 1)
                                    prep.dve(dve)
                                    prep.gate_dve(dve)
                                    dve.wait_ge(s.g_done, 1)
                                    dve.wait_ge(s.extra_in, 16)
                                    for h in range(2):
                                        half = gate[:, :, h * HD:(h + 1) * HD]
                                        nc.vector.tensor_tensor(half, half, par[:, 1:].unsqueeze(1).to_broadcast([P, TILES, HD]),
                                                                ALU.mult).then_inc(s.extra, 1)
                                    dve.wait_ge(s.extra, 2)
                                    for kind, n, m, c in steps:
                                        w = width(n, c)
                                        h, i = items[n]
                                        z = n % 2
                                        if kind == "max":
                                            a = index[n, m, c]
                                            dve.wait_ge(s.mx, a + 1)
                                            nc.vector.reduce_max(chunk_max[:, z, m, c:c + 1], ps[:, a % 2, 0:w], AX).then_inc(s.rmax, 1)
                                        elif kind == "shift":
                                            dve.wait_ge(s.rmax, index[n, m, nch[n] - 1] + 1)
                                            if n >= 2:
                                                dve.wait_ge(s.cmax, index[n - 2, m, nch[n - 2] - 1] + 1)
                                            nc.vector.reduce_max(shift[:, z, m, 0:1], chunk_max[:, z, m, 0:nch[n]], AX).then_inc(s.extra, 1)
                                            dve.wait_ge(s.extra, 2 + 2 * n + m + 1)
                                            nc.vector.tensor_scalar(shift[:, z, m, 1:2], shift[:, z, m, 0:1], -DA_SCALE, None,
                                                                    ALU.mult).then_inc(s.sm, 1)
                                        elif kind == "ratio":
                                            dve.wait_ge(s.cmax, index[n, 1, nch[n] - 1] + 1)
                                            nc.vector.reduce_sum(sums[:, n % 8, 0:2], part_sum[:, z, :, 0:nch[n]], AX).then_inc(s.tot, 1)
                                            dve.wait_ge(s.tot, n + 1)
                                            nc.vector.reciprocal(sums[:, n % 8, 2:4], sums[:, n % 8, 0:2]).then_inc(s.rec, 1)
                                            dve.wait_ge(s.rec, n + 1)
                                            nc.vector.scalar_tensor_tensor(out=sums[:, n % 8, 4:5], in0=sums[:, n % 8, 0:1], scalar=par[:, 0:1],
                                                                           in1=sums[:, n % 8, 3:4], op0=ALU.mult,
                                                                           op1=ALU.mult).then_inc(s.ratio, 1)
                                        elif kind == "weigh":
                                            dve.wait_ge(s.ratio, n + 1)
                                            keys = slice(N * c, N * c + w)
                                            nc.vector.scalar_tensor_tensor(out=ex[:, z, 0, keys], in0=ex[:, z, 1, keys],
                                                                           scalar=sums[:, n % 8, 4:5], in1=ex[:, z, 0, keys],
                                                                           op0=ALU.mult, op1=ALU.add).then_inc(s.wg, 1)
                                        elif kind == "copy" and uindex[n, c] % 2 == 1:
                                            u = uindex[n, c]
                                            dve.wait_ge(s.wtr, u + 1)
                                            if u >= 4:
                                                dve.wait_ge(s.av, u - 3)
                                            nc.vector.tensor_copy(wt[:, u % 4, 0:w], ps[:, 6, 0:w]).then_inc(s.wt_dve, 1)
                                        elif kind == "norm":
                                            dve.wait_ge(s.av, uindex[n, nch[n] - 1] + 1)
                                            nc.vector.tensor_scalar(o1[:, n % 4], ps[:, 7, 0:HD], sums[:, n % 8, 2:3], None,
                                                                    ALU.mult).then_inc(s.o1, 1)
                                            dve.wait_ge(s.o1, n + 1)
                                            nc.vector.tensor_tensor_reduce(o2[:, n % 4], o1[:, n % 4], o1[:, n % 4], 1.0, 0.0, ALU.mult, ALU.add,
                                                                           norm[:, n % 4, 0:1]).then_inc(s.ss, 1)
                                        elif kind == "gated":
                                            cols = slice(h * HD, (h + 1) * HD)
                                            dve.wait_ge(s.rs, n + 1)
                                            nc.vector.scalar_tensor_tensor(out=ybuf[:, i, cols], in0=o1[:, n % 4], scalar=norm[:, n % 4, 1:2],
                                                                           in1=gate[:, i, cols], op0=ALU.mult,
                                                                           op1=ALU.mult).then_inc(s.y, 1)

                                @block.tensor
                                def _(pe):
                                    prep.pe(pe)

                                    def scores(bank, n, m, c):
                                        h, i = items[n]
                                        w = width(n, c)
                                        out_ = ps[:, bank, 0:w]
                                        own = c == nch[n] - 1
                                        last = nc.tensor.matmul(out_, operand[:, 4 * h + 2 * m, i * P:(i + 1) * P],
                                                                operand[:, 4 * h + 2 * m + 1, N * c:N * c + w], start=True, stop=not own,
                                                                skip_group_check=own)
                                        if own:
                                            last = nc.tensor.matmul(ps[:, bank, w - P:w], identb[:, :], chunk_mask[:, :],
                                                                    start=False, stop=True, skip_group_check=True)
                                        return last

                                    for kind, n, m, c in steps:
                                        w = width(n, c)
                                        if kind == "max":
                                            a = index[n, m, c]
                                            if a >= 2:
                                                pe.wait_ge(s.rmax, a - 1)
                                            scores(a % 2, n, m, c).then_inc(s.mx, 1)
                                        elif kind == "exp":
                                            a = index[n, m, c]
                                            if a >= 3:
                                                pe.wait_ge(s.cmax, a - 2)
                                            scores(2 + a % 3, n, m, c).then_inc(s.ex, 1)
                                        elif kind == "turn":
                                            u = uindex[n, c]
                                            pe.wait_ge(s.wg, u + 1)
                                            if u >= 2:
                                                pe.wait_ge((s.wt_act, s.wt_dve)[u % 2], u // 2)
                                            for b in range(w // P):
                                                last = nc.tensor.transpose(ps[:, 5 + u % 2, b * P:(b + 1) * P],
                                                                           ex[:, n % 2, 0, N * c + b * P:N * c + (b + 1) * P],
                                                                           ident[:, :])
                                            last.then_inc(s.wtr, 1)
                                        elif kind == "value":
                                            u = uindex[n, c]
                                            h = items[n][0]
                                            pe.wait_ge((s.wt_act, s.wt_dve)[u % 2], u // 2 + 1)
                                            if c == 0 and n >= 1:
                                                pe.wait_ge(s.o1, n)
                                            for b in range(w // P):
                                                last = nc.tensor.matmul(ps[:, 7, 0:HD], wt[:, u % 4, b * P:(b + 1) * P],
                                                                        val[:, 4 * c + b, h * HD:(h + 1) * HD],
                                                                        start=(c == 0 and b == 0),
                                                                        stop=(c == nch[n] - 1 and b == w // P - 1))
                                            last.then_inc(s.av, 1)

            with ExitStack() as scope, phase("gain_in", "w_in0", "w_in1", "w_hi", "w_lo", "y_in0", "y_in1",
                                             "x_in0", "x_in1", "x_in2", "yt", "hi", "lo", "acc",
                                             "sq", "ms", "rstd", "sc", "res", "next0", "next1", "next2",
                                             "out0", "out1", "out2") as s:
                w_ins, y_ins, x_ins = (s.w_in0, s.w_in1), (s.y_in0, s.y_in1), (s.x_in0, s.x_in1, s.x_in2)
                nexts, outs = (s.next0, s.next1, s.next2), (s.out0, s.out1, s.out2)
                gain = sb("post", [P, D], F32, scope)
                w_raw = sb("wo_raw", [P, 2, D], F32, scope)
                w_hi = sb("wo_hi", [P, KC, D], F32R, scope)
                w_lo = sb("wo_lo", [P, KC, D], F32R, scope)
                yt = sb("yt", [P, 2, D], F32, scope)
                xt = sb("xo", [P, 3, D], F32, scope)
                y_hi = sb("y_hi", [P, 2, KC, P], F32R, scope)
                y_lo = sb("y_lo", [P, 2, KC, P], F32R, scope)
                z = sb("z", [P, 3, D], F32, scope)
                st = sb("sto", [P, 2, 2], F32, scope)
                with nc.Block() as block:
                    @block.sync
                    def _(sp):
                        sp.dma_start(gain[:, :], post_gain[layer].unsqueeze(0).to_broadcast([P, D])).then_inc(s.gain_in, 16)
                        for k in range(KC):
                            if k >= 2:
                                sp.wait_ge(s.w_lo, k - 1)
                            sp.dma_start(w_raw[:, k % 2], w_out[layer, k * P:(k + 1) * P, :]).then_inc(w_ins[k % 2], 16)
                            if k < 2:
                                sp.dma_start(yt[:, k], ymix[k * P:(k + 1) * P, :]).then_inc(y_ins[k], 16)
                                sp.dma_start(xt[:, k], xs[layer, k * P:(k + 1) * P, :]).then_inc(x_ins[k], 16)
                        for t in range(TILES):
                            if 2 <= t + 2 < TILES:
                                r = t + 2
                                sp.wait_ge(s.yt, r - 1)
                                sp.dma_start(yt[:, r % 2], ymix[r * P:(r + 1) * P, :]).then_inc(y_ins[r % 2], 16)
                                if r >= 3:
                                    sp.wait_ge(s.res, r - 2)
                                sp.dma_start(xt[:, r % 3], xs[layer, r * P:(r + 1) * P, :]).then_inc(x_ins[r % 3], 16)
                            sp.wait_ge(s.res, t + 1)
                            sp.dma_start(xs[layer + 1, t * P:(t + 1) * P, :], z[:, t % 3]).then_inc(nexts[t % 3], 16)
                            sp.dma_start(out[t * P:(t + 1) * P, :], z[:, t % 3]).then_inc(outs[t % 3], 16)
                        for j in range(3):
                            sp.wait_ge(nexts[j], 16 * len(range(j, TILES, 3)))
                            sp.wait_ge(outs[j], 16 * len(range(j, TILES, 3)))

                    @block.scalar
                    def _(act):
                        act.preload_act_table_set(EXP_LN)
                        for k in range(KC):
                            act.wait_ge(w_ins[k % 2], 16 * (k // 2 + 1))
                            nc.scalar.activation(w_hi[:, k], w_raw[:, k % 2], ACT.Copy).then_inc(s.w_hi, 1)
                        for t in range(TILES + 1):
                            if t < TILES:
                                act.wait_ge(s.yt, t + 1)
                                if t >= 2:
                                    act.wait_ge(s.acc, t - 1)
                                for j in range(2):
                                    nc.scalar.activation(y_hi[:, t % 2, 4 * j:4 * j + 4].rearrange("p k n -> p (k n)"),
                                                         ps[:, 2 * (t % 2) + j, :], ACT.Copy).then_inc(s.hi, 1)
                            if t >= 1:
                                m = t - 1
                                act.wait_ge(s.acc, t)
                                if m >= 3:
                                    act.wait_ge(nexts[m % 3], 16 * (m // 3))
                                    act.wait_ge(outs[m % 3], 16 * (m // 3))
                                b = 4 + 2 * (m % 2)
                                nc.scalar.activation(z[:, m % 3], ps[:, b:b + 2, :].rearrange("p b n -> p (b n)"), ACT.Square,
                                                     accum_out=st[:, m % 2, 0:1]).then_inc(s.sq, 1)
                                act.wait_ge(s.sq, t)
                                nc.scalar.activation(st[:, m % 2, 1:2], st[:, m % 2, 0:1], ACT.Ln, scale=1.0 / D,
                                                     bias=eps[:, :]).then_inc(s.ms, 1)
                                act.wait_ge(s.ms, t)
                                nc.scalar.activation(st[:, m % 2, 1:2], st[:, m % 2, 1:2], ACT.Exp, scale=-0.5).then_inc(s.rstd, 1)

                    @block.vector
                    def _(dve):
                        for k in range(KC):
                            dve.wait_ge(s.w_hi, k + 1)
                            nc.vector.tensor_tensor(w_lo[:, k], w_raw[:, k % 2], w_hi[:, k].bitcast(F32), ALU.subtract).then_inc(s.w_lo, 1)
                        dve.wait_ge(s.gain_in, 16)
                        for t in range(TILES + 1):
                            if t < TILES:
                                for j in range(2):
                                    dve.wait_ge(s.hi, 2 * t + j + 1)
                                    hs = y_hi[:, t % 2, 4 * j:4 * j + 4].rearrange("p k n -> p (k n)")
                                    nc.vector.tensor_tensor(y_lo[:, t % 2, 4 * j:4 * j + 4].rearrange("p k n -> p (k n)"),
                                                            ps[:, 2 * (t % 2) + j, :], hs.bitcast(F32), ALU.subtract).then_inc(s.lo, 1)
                            if t >= 1:
                                m = t - 1
                                dve.wait_ge(s.rstd, t)
                                b = 4 + 2 * (m % 2)
                                nc.vector.scalar_tensor_tensor(out=z[:, m % 3], in0=ps[:, b:b + 2, :].rearrange("p b n -> p (b n)"),
                                                               scalar=st[:, m % 2, 1:2], in1=gain[:, :], op0=ALU.mult,
                                                               op1=ALU.mult).then_inc(s.sc, 1)
                                dve.wait_ge(s.sc, t)
                                dve.wait_ge(x_ins[m % 3], 16 * (m // 3 + 1))
                                nc.vector.tensor_tensor(z[:, m % 3], z[:, m % 3], xt[:, m % 3], ALU.add).then_inc(s.res, 1)

                    @block.tensor
                    def _(pe):
                        for t in range(TILES + 1):
                            if t < TILES:
                                pe.wait_ge(y_ins[t % 2], 16 * (t // 2 + 1))
                                if t >= 2:
                                    pe.wait_ge(s.lo, 2 * (t - 1))
                                for k in range(KC):
                                    last = nc.tensor.transpose(ps[:, 2 * (t % 2) + k // 4, (k % 4) * P:(k % 4 + 1) * P],
                                                               yt[:, t % 2, k * P:(k + 1) * P], ident[:, :])
                                last.then_inc(s.yt, 1)
                            if t >= 1:
                                m = t - 1
                                if m == 0:
                                    pe.wait_ge(s.w_lo, KC)
                                pe.wait_ge(s.lo, 2 * t)
                                if m >= 2:
                                    pe.wait_ge(s.sc, m - 1)
                                for half in range(D // N):
                                    acc = ps[:, 4 + 2 * (m % 2) + half, :]
                                    cols = slice(half * N, (half + 1) * N)
                                    for k in range(KC):
                                        nc.tensor.matmul(acc, y_hi[:, m % 2, k], w_hi[:, k, cols], start=(k == 0), stop=False)
                                        nc.tensor.matmul(acc, y_hi[:, m % 2, k], w_lo[:, k, cols], start=False, stop=False)
                                        last = nc.tensor.matmul(acc, y_lo[:, m % 2, k], w_hi[:, k, cols], start=False,
                                                                stop=(k == KC - 1))
                                last.then_inc(s.acc, 1)


def pair_columns():
    cols = []
    base = 0
    for width in (384, 384, 256):
        for p in range(width // 128):
            for part in range(4):
                at = base + part * width + p * 128
                cols.extend(range(at, at + 128))
        base += 4 * width
    return cols


def kernel(x, positions, w_in, w_out, pre_gain, post_gain, rel_bias, lambda_q1, lambda_k1, lambda_q2,
           lambda_k2, subln_gain):
    import concourse.bacc as bacc
    from concourse.bass_utils import run_bass_kernel_spmd

    w_in = np.asarray(w_in)
    depth, d, wide = w_in.shape
    w_pairs = w_in[:, :, pair_columns()].reshape(depth, d // 128, 128, wide // 512, 512).transpose(0, 3, 2, 1, 4)
    arrays = {"x": np.asarray(x)[0], "positions": np.asarray(positions)[0], "w_pairs": w_pairs, "w_out": w_out,
              "pre_gain": pre_gain, "post_gain": post_gain, "rel_bias": rel_bias, "lq1": lambda_q1, "lk1": lambda_k1,
              "lq2": lambda_q2, "lk2": lambda_k2, "subln_gain": subln_gain}
    arrays = {f"in_{k}": np.ascontiguousarray(a) for k, a in arrays.items()}
    nc = bacc.Bacc("TRN2", target_bir_lowering=False, num_devices=1)
    args = {k[3:]: nc.dram_tensor(k, a.shape, mybir.dt.from_np(a.dtype), kind="ExternalInput").ap() for k, a in arrays.items()}
    out = nc.dram_tensor("out", arrays["in_x"].shape, F32, kind="ExternalOutput").ap()
    trunk(nc, out=out, **args)
    r = run_bass_kernel_spmd(nc, [arrays], core_ids=[0])
    return r.results[0]["out"][None]
```
